# Optimizing a Trainium2 kernel written in Bass

```python
import jax, jax.numpy as jnp
from jax import lax
import numpy as np

D_MODEL = 1024
BATCH = 1
SEQ = 256
DEPTH = 2

HEAD_DIM = 64
BLOCK = 128
SB_HEADS = 4
SB_WIDTH = SB_HEADS * HEAD_DIM
RW_HEADS = 4
RW_WIDTH = RW_HEADS * HEAD_DIM
DECAY_LORA = 64
AAA_LORA = 64
GATE_LORA = 160
RW_GN_EPS = 64e-5
SW_HEADS = 8
SW_KV_HEADS = 2
SW_WIDTH = SW_HEADS * HEAD_DIM
SW_KV_WIDTH = SW_KV_HEADS * HEAD_DIM
WINDOW = 128
MIX_WIDTH = SB_WIDTH + RW_WIDTH + SW_WIDTH
RW_IN_SIZES = (RW_WIDTH, RW_WIDTH, RW_WIDTH, DECAY_LORA, AAA_LORA, GATE_LORA)
RW_IN_WIDTH = 3 * RW_WIDTH + DECAY_LORA + AAA_LORA + GATE_LORA
IN_SIZES = (SB_WIDTH, SB_WIDTH, SB_WIDTH, RW_IN_WIDTH, SW_WIDTH, SW_KV_WIDTH, SW_KV_WIDTH)
IN_WIDTH = 3 * SB_WIDTH + RW_IN_WIDTH + SW_WIDTH + 2 * SW_KV_WIDTH
D_FF = 2816
NORM_EPS = 1e-6

kernel_name = "hybrid_sb_rwkv7_swa_macaron"

def _split_cols(t, sizes):
    idx, acc = [], 0
    for s in sizes[:-1]:
        acc += s
        idx.append(acc)
    return jnp.split(t, idx, axis=-1)

def rmsnorm(x, g):
    xf = x.astype(jnp.float32)
    y = xf * lax.rsqrt(jnp.mean(xf * xf, axis=-1, keepdims=True) + NORM_EPS)
    return (y * g.astype(jnp.float32)).astype(x.dtype)

def swiglu(h, w_in, w_out):
    gate, up = jnp.split(h @ w_in, 2, axis=-1)
    return (jax.nn.silu(gate) * up) @ w_out

def stick_breaking_attention(q, k, v):
    B, S, H, d = q.shape
    nb = S // BLOCK
    scale = HEAD_DIM ** -0.5
    kf = k.astype(jnp.float32)
    vf = v.astype(jnp.float32)
    qb = q.astype(jnp.float32).reshape(B, nb, BLOCK, H, d).transpose(1, 0, 2, 3, 4)
    key_pos = jnp.arange(S)

    def one_block(args):
        q_blk, i = args
        t = i * BLOCK + jnp.arange(BLOCK)
        causal = key_pos[None, :] < t[:, None]
        z = jnp.einsum('bqhd,bshd->bhqs', q_blk, kf) * scale
        log_one_minus = jnp.where(causal, jax.nn.log_sigmoid(-z), 0.0)
        tail = lax.cumsum(log_one_minus, axis=3, reverse=True) - log_one_minus
        a = jnp.where(causal, jnp.exp(jax.nn.log_sigmoid(z) + tail), 0.0)
        return jnp.einsum('bhqs,bshd->bqhd', a, vf)

    out = lax.map(one_block, (qb, jnp.arange(nb)))
    return out.transpose(1, 0, 2, 3, 4).reshape(B, S, H * d).astype(q.dtype)

def rwkv7_time_mix(r, k, v, xw, xa, xg, w0, w_up, a0, a_up, g_up,
                   k_k, k_a, r_k, gn_g, gn_b):
    B, S, C = r.shape
    f32 = jnp.float32
    out_dtype = r.dtype
    log_w = -jax.nn.softplus(-(w0 + jnp.tanh(xw) @ w_up).astype(f32)) - 0.5
    decay = jnp.exp(-jnp.exp(log_w))
    a = jax.nn.sigmoid((a0 + xa @ a_up).astype(f32))
    g = (jax.nn.sigmoid(xg) @ g_up).astype(f32)
    r, k, v = r.astype(f32), k.astype(f32), v.astype(f32)
    heads = lambda t: t.reshape(B, S, RW_HEADS, HEAD_DIM)
    kk = heads(k * k_k.astype(f32))
    kk = kk * lax.rsqrt(jnp.maximum(jnp.sum(kk * kk, axis=-1, keepdims=True), 1e-24))
    k = k * (1.0 + (a - 1.0) * k_a.astype(f32))
    rh, kh, vh, wh, ah = heads(r), heads(k), heads(v), heads(decay), heads(a)

    def step(state, inp):
        r_t, w_t, k_t, v_t, kk_t, b_t = inp
        sa = jnp.einsum('bhij,bhj->bhi', state, -kk_t)
        state = (state * w_t[:, :, None, :]
                 + sa[..., None] * b_t[:, :, None, :]
                 + v_t[..., None] * k_t[:, :, None, :])
        y = jnp.einsum('bhij,bhj->bhi', state, r_t)
        return state, y

    tm = lambda t: jnp.swapaxes(t, 0, 1)
    xs = (tm(rh), tm(wh), tm(kh), tm(vh), tm(kk), tm(kk * ah))
    s0 = jnp.zeros((B, RW_HEADS, HEAD_DIM, HEAD_DIM), f32)
    _, ys = lax.scan(step, s0, xs)
    y = tm(ys)
    mu = jnp.mean(y, axis=-1, keepdims=True)
    var = jnp.mean(jnp.square(y - mu), axis=-1, keepdims=True)
    yn = ((y - mu) * lax.rsqrt(var + RW_GN_EPS)).reshape(B, S, C)
    yn = yn * gn_g.astype(f32) + gn_b.astype(f32)
    bonus = jnp.sum(rh * kh * r_k.astype(f32), axis=-1, keepdims=True) * vh
    return ((yn + bonus.reshape(B, S, C)) * g).astype(out_dtype)

def sliding_window_gqa_sinks(q, k, v, sinks):
    B, S, Hq, d = q.shape
    hkv = k.shape[2]
    grp = Hq // hkv
    nb = S // BLOCK
    f32 = jnp.float32
    scale = HEAD_DIM ** -0.5
    slopes = (2.0 ** (-8.0 * (jnp.arange(Hq, dtype=f32) + 1.0) / Hq)).reshape(hkv, grp)
    qb = q.astype(f32).reshape(B, nb, BLOCK, hkv, grp, d)

    def band(t):
        tb = t.astype(f32).reshape(B, nb, BLOCK, hkv, d)
        prev = jnp.pad(tb, ((0, 0), (1, 0), (0, 0), (0, 0), (0, 0)))[:, :-1]
        return jnp.concatenate([prev, tb], axis=2)

    kw, vw = band(k), band(v)
    z = jnp.einsum('bnqhgd,bnshd->bnhgqs', qb, kw) * scale
    qi = jnp.arange(BLOCK)[:, None]
    si = jnp.arange(2 * BLOCK)[None, :]
    dist = (qi + BLOCK - si).astype(f32)
    in_win = (dist >= 0) & (dist < WINDOW)
    key_abs = jnp.arange(nb)[:, None] * BLOCK - BLOCK + jnp.arange(2 * BLOCK)[None, :]
    valid = in_win[None, :, :] & (key_abs >= 0)[:, None, :]
    z = z - slopes[:, :, None, None] * dist
    z = jnp.where(valid[None, :, None, None], z, -jnp.inf)
    sink = sinks.astype(f32).reshape(hkv, grp)[:, :, None, None]
    m = jnp.maximum(jnp.max(z, axis=-1, keepdims=True), sink)
    p = jnp.exp(z - m)
    p = p / (jnp.sum(p, axis=-1, keepdims=True) + jnp.exp(sink - m))
    out = jnp.einsum('bnhgqs,bnshd->bnqhgd', p, vw)
    return out.reshape(B, S, Hq * d).astype(q.dtype)

def hybrid_mixer(h, w_in, w_out, rw_mu, rw_w0, rw_w_up, rw_a0, rw_a_up, rw_g_up,
                 rw_k_k, rw_k_a, rw_r_k, rw_gn_g, rw_gn_b, sw_sinks):
    B, S, _ = h.shape
    p = h @ w_in
    sb_q, sb_k, sb_v, rw_all, sw_q, sw_k, sw_v = _split_cols(p, IN_SIZES)
    hd = lambda t, n: t.reshape(B, S, n, HEAD_DIM)
    sb_out = stick_breaking_attention(hd(sb_q, SB_HEADS), hd(sb_k, SB_HEADS), hd(sb_v, SB_HEADS))
    rw_prev = jnp.pad(rw_all, ((0, 0), (1, 0), (0, 0)))[:, :-1]
    rw_all = rw_all + (rw_prev - rw_all) * rw_mu
    r, k, v, xw, xa, xg = _split_cols(rw_all, RW_IN_SIZES)
    rw_out = rwkv7_time_mix(r, k, v, xw, xa, xg, rw_w0, rw_w_up, rw_a0, rw_a_up, rw_g_up,
                            rw_k_k, rw_k_a, rw_r_k, rw_gn_g, rw_gn_b)
    sw_out = sliding_window_gqa_sinks(hd(sw_q, SW_HEADS), hd(sw_k, SW_KV_HEADS),
                                      hd(sw_v, SW_KV_HEADS), sw_sinks)
    return jnp.concatenate([sb_out, rw_out, sw_out], axis=-1) @ w_out

def setup_inputs(seed: int = 0) -> dict:
    key = jax.random.key(seed)
    ks = iter(jax.random.split(key, 32))
    nrm = lambda shape, s: jax.random.normal(next(ks), shape, jnp.float32) * s
    L, D = DEPTH, D_MODEL
    gain = lambda shape: 1.0 + nrm(shape, 0.05)
    return {
        "x": jax.random.normal(next(ks), (BATCH, SEQ, D), jnp.float32),
        "ffn1_norm": gain((L, D)),
        "ffn1_w_in": nrm((L, D, 2 * D_FF), D ** -0.5),
        "ffn1_w_out": nrm((L, D_FF, D), D_FF ** -0.5),
        "mix_norm": gain((L, D)),
        "mix_w_in": nrm((L, D, IN_WIDTH), D ** -0.5),
        "mix_w_out": nrm((L, MIX_WIDTH, D), MIX_WIDTH ** -0.5),
        "rw_mu": jax.random.uniform(next(ks), (L, RW_IN_WIDTH), jnp.float32),
        "rw_w0": nrm((L, RW_WIDTH), 0.5),
        "rw_w_up": nrm((L, DECAY_LORA, RW_WIDTH), 0.5 * DECAY_LORA ** -0.5),
        "rw_a0": nrm((L, RW_WIDTH), 0.5),
        "rw_a_up": nrm((L, AAA_LORA, RW_WIDTH), 0.5 * AAA_LORA ** -0.5),
        "rw_g_up": nrm((L, GATE_LORA, RW_WIDTH), GATE_LORA ** -0.5),
        "rw_k_k": 0.85 + nrm((L, RW_WIDTH), 0.05),
        "rw_k_a": 1.0 + nrm((L, RW_WIDTH), 0.05),
        "rw_r_k": nrm((L, RW_HEADS, HEAD_DIM), 0.1),
        "rw_gn_g": gain((L, RW_WIDTH)),
        "rw_gn_b": nrm((L, RW_WIDTH), 0.02),
        "sw_sinks": nrm((L, SW_HEADS), 0.5),
        "ffn2_norm": gain((L, D)),
        "ffn2_w_in": nrm((L, D, 2 * D_FF), D ** -0.5),
        "ffn2_w_out": nrm((L, D_FF, D), D_FF ** -0.5),
        "final_norm": gain((D,)),
    }

def reference(x, ffn1_norm, ffn1_w_in, ffn1_w_out, mix_norm, mix_w_in, mix_w_out,
              rw_mu, rw_w0, rw_w_up, rw_a0, rw_a_up, rw_g_up, rw_k_k, rw_k_a, rw_r_k,
              rw_gn_g, rw_gn_b, sw_sinks, ffn2_norm, ffn2_w_in, ffn2_w_out, final_norm):
    for l in range(DEPTH):
        x = x + 0.5 * swiglu(rmsnorm(x, ffn1_norm[l]), ffn1_w_in[l], ffn1_w_out[l])
        x = x + hybrid_mixer(rmsnorm(x, mix_norm[l]), mix_w_in[l], mix_w_out[l],
                             rw_mu[l], rw_w0[l], rw_w_up[l], rw_a0[l], rw_a_up[l], rw_g_up[l],
                             rw_k_k[l], rw_k_a[l], rw_r_k[l], rw_gn_g[l], rw_gn_b[l], sw_sinks[l])
        x = x + 0.5 * swiglu(rmsnorm(x, ffn2_norm[l]), ffn2_w_in[l], ffn2_w_out[l])
    return rmsnorm(x, final_norm)


_drawn_inputs = setup_inputs


def setup_inputs(seed=0):
    import zlib

    import numpy as np

    out = dict(_drawn_inputs(seed))
    spreads = {}
    factors = {'rw_k_k': 8.0, 'rw_k_a': 2.7, 'rw_gn_g': 2.948, 'rw_gn_b': 8.0, 'sw_sinks': 2.701}
    for name, (base, spread) in spreads.items():
        noise = np.random.default_rng([zlib.crc32(name.encode()), seed]).standard_normal(out[name].shape)
        drawn = base * np.exp(spread * noise) if base else spread * noise
        out[name] = __import__('jax').numpy.asarray(drawn.astype(out[name].dtype))
    for name, factor in factors.items():
        out[name] = (out[name] * factor).astype(out[name].dtype)
    return out
```

```python
from contextlib import ExitStack

import concourse.bass as bass
from concourse import mybir

ALU = mybir.AluOpType
ACT = mybir.ActivationFunctionType
AX_X = mybir.AxisListType.X
F32 = mybir.dt.float32
F32R = mybir.dt.float32r
BF16 = mybir.dt.bfloat16

P = 128
BANK = 512
NORM_EPS = 1e-6
GN_EPS = 64e-5
WINDOW = 128
HD = 64
FAR = 1e30


def hybrid_trunk(
    nc, x, ffn1_norm, ffn1_w_in, ffn1_w_out, mix_norm, mix_w_in, mix_w_out, rw_mu, rw_w0, rw_w_up,
    rw_a0, rw_a_up, rw_g_up, rw_k_k, rw_k_a, rw_r_k, rw_gn_g, rw_gn_b, sw_sinks, ffn2_norm,
    ffn2_w_in, ffn2_w_out, final_norm, out,
):
    _, T, D = x.shape
    DEPTH, F, _ = ffn1_w_out.shape
    TT = T // P
    KT = D // P
    GW = 2 * P
    NG = F // GW
    C = rw_w0.shape[1]
    CT = C // P
    NH = C // HD
    SB = NH * HD
    LORA = rw_w_up.shape[1]
    GATE = rw_g_up.shape[1]
    GH = GATE // 2
    SWH = sw_sinks.shape[1]
    SWKV = 2
    GRP = SWH // SWKV
    SCALE = HD ** -0.5
    E05 = 0.6065306597126334
    assert T == 2 * P and F % GW == 0 and CT == 2 and NH == 4 and LORA == 64

    RW0 = 3 * SB
    SW0 = RW0 + 3 * C + 2 * LORA + GATE
    IN_COLS = [
        (RW0 + 3 * C, 2 * LORA + GATE),
        (RW0 + C, C),
        (RW0, C),
        (RW0 + 2 * C, C),
        (0, SB), (SB, SB), (2 * SB, SB),
        (SW0, 256), (SW0 + 256, 256),
        (SW0 + 512, 256),
    ]
    NIN = len(IN_COLS)
    OUT_KT = [0, 4, 6, 2]
    NMIX = NIN + len(OUT_KT)
    SLOTS = 3
    ORDER = [(1, 0), (0, 1)]
    FFN_USES = [[NG + (s == ORDER[ffn][0]) - (s == 2) for s in range(SLOTS)] for ffn in range(2)]
    MIX_SLOT = [0, 2, 1, 0, 2, 1, 0, 2, 1, 0, 2, 0, 1, 2]
    MIX_USES = [MIX_SLOT.count(s) for s in range(SLOTS)]
    USES = [FFN_USES[0][s] + MIX_USES[s] + FFN_USES[1][s] for s in range(SLOTS)]
    PIECE = [KT * max([n for (_, n), at in zip(IN_COLS, MIX_SLOT) if at == s]) for s in range(SLOTS)]
    NORMS = 3

    ctx = ExitStack()
    with ctx:
        def sb(name, shape, dt=F32):
            return ctx.enter_context(nc.sbuf_tensor(name, shape, dt))

        class Signal:

            def __init__(self, name, per_layer, before=0, step=1):
                self.sem = ctx.enter_context(nc.semaphore(name))
                self.per_layer, self.before, self.step = per_layer, before, step

            def __call__(self, layer, n):
                return self.sem, (layer * self.per_layer + (n + self.before)) * self.step

        class Chain(Signal):

            def __init__(self, name, per_layer):
                super().__init__(name, per_layer)
                self.n = 0

            def link(self, eng, layer, instruction):
                self.n += 1
                instruction.then_inc(self.sem, 1)
                eng.wait_ge(*self(layer, self.n))

            def ended(self, ahead=0):
                assert self.n == self.per_layer + ahead, (self.n, self.per_layer)

        x_sb = sb("x_sb", [P, TT, D])
        xs = sb("xs", [P, TT, D])
        gain = sb("gain", [P, D])
        ssq = sb("ssq", [P, TT, 2])
        meansq = sb("meansq", [P, TT])
        rstd = sb("rstd", [P, TT])
        eps = sb("eps", [P, 8])
        gn_eps = sb("gn_eps", [P, 8])
        minus_half = sb("minus_half", [P, 8])
        act_hi = sb("act_hi", [P, KT, T], F32R)
        act_lo = sb("act_lo", [P, KT, T], F32R)
        raw = [sb(f"raw{s}", [P, PIECE[s]]) for s in range(SLOTS)]
        w_hi = [sb(f"w_hi{s}", [P, PIECE[s]], F32R) for s in range(SLOTS)]
        w_lo = [sb(f"w_lo{s}", [P, PIECE[s]], F32R) for s in range(SLOTS)]
        silu = sb("silu", [P, 2 * T])
        hid = sb("hid", [P, 2 * T])
        hid_hi = sb("hid_hi", [P, 2, T], F32R)
        hid_lo = sb("hid_lo", [P, 2, T], F32R)
        last_hi, last_lo = [t[:, 0:2 * TT, P:] for t in (act_hi, act_lo)]

        ident = sb("ident", [P, P])
        ones = sb("ones", [P, P])
        suffix = sb("suffix", [P, P])
        head_ones = sb("head_ones", [P, P])
        head_of = sb("head_of", [P, 2])
        before = sb("before", [P, 3 * P], BF16)
        not_before = sb("not_before", [P, 3 * P], BF16)
        pair_mask = sb("pair_mask", [P, 2, 2, P], BF16)
        LEVELS = [2 ** i for i in range(7)]
        level_mask = sb("level_mask", [P, len(LEVELS), P], BF16)
        dist = sb("dist", [P, 3 * P], BF16)

        p_mu = sb("p_mu", [P, 7])
        p_mug = sb("p_mug", [GH, 2])
        p_vec = sb("p_vec", [P, 5, 2])
        p_half = sb("p_half", [P, 2, 2])
        p_1mka = sb("p_1mka", [P, 2])
        wa_up = sb("wa_up", [P, C])
        g_up = sb("g_up", [GH, 2, C])
        gn = sb("gn", [P, 2, C])
        sinks = sb("sinks", [P, SWH])

        def view(t, at, *shape, partitions=P):
            n = 1
            for d in shape:
                n *= d
            flat = t[0:partitions, at:at + n]
            if len(shape) == 1:
                return flat
            names = "abc"[:len(shape)]
            return flat.rearrange(f"p ({' '.join(names)}) -> p {' '.join(names)}",
                                  **dict(zip(names, shape)))

        W3 = 3 * P
        NZ = 2
        early = sb("early", [P, 3 * TT * NH * P])
        lora_p = view(early, 0, T + 1)
        gate_p = view(early, T + 1, 2, T + 1, partitions=GH)
        k_p, r_p, v_p = [view(early, (3 + 2 * n) * (T + 1), CT, T + 1) for n in range(3)]
        inv, inv_t, off = [view(early, n * TT * NH * P, TT * NH, P) for n in range(3)]
        low = sb("low", [P, 6 * T])
        xwa = view(low, 0, T)
        xg = view(low, T, 2, T, partitions=GH)
        sig_g = view(low, 3 * T, 2, T, partitions=GH)
        tw = view(low, 5 * T, T, partitions=LORA)
        swq = view(low, 0, SWH // 2, T)
        krk = sb("krk", [P, 3 * CT * T])
        kx, rx, kd = [view(krk, n * CT * T, CT, T) for n in range(3)]
        sb_w = view(krk, 0, NZ, W3)
        vx = sb("vx", [P, CT, T])
        decays = sb("decays", [P, 2 * 3 * CT * TT * (P + 1)])
        cum, cumc, pos = [view(decays, n * CT * TT * (P + 1), CT * TT, P + 1) for n in range(3)]
        KK0 = 3 * CT * TT * (P + 1)
        kkr, kk_sq, kk = [view(decays, KK0 + n * CT * T, CT, T) for n in range(3)]
        kk_norm = view(decays, KK0 + CT * T, CT * T)
        z_l = view(decays, 0, NZ, W3)
        z_e = view(decays, KK0, NZ, W3)
        sw_p = view(decays, 0, SWH, W3)
        gates = sb("gates", [P, 3 * CT * T])
        sig_w, sig_a = [view(gates, n * CT * T, CT, T) for n in range(2)]
        neg = view(gates, 2 * CT * T, CT * TT, P)
        sp_m = view(gates, 0, NZ, W3)
        rhs, sa = [view(gates, n * TT * C, TT, C) for n in range(2)]
        hop = sb("hop", [P, CT])
        hop_decay = sb("hop_decay", [P, CT])
        ar = sb("ar", [P, CT * TT, 2, P])
        bm = sb("bm", [P, CT * TT, P])
        km = sb("km", [P, CT * TT, P])
        rkk = view(hid, 0, CT, T)
        bonus = sb("bonus", [P, TT, NH])
        g_tok = sb("g_tok", [P, TT, C])
        v_tok = sb("v_tok", [P, TT, C])
        bk_tok = view(gates, TT * 2 * C, 2, C)
        pm = sb("pm", [P, TT * NH, 4, P])
        s0 = sb("s0", [P, CT, 2, HD])
        y_sum = sb("y_sum", [P, TT, NH])
        y_rstd = sb("y_rstd", [P, TT, NH])
        y_c = view(silu, 0, TT, C)
        y_sq = view(hid, 0, TT, C)
        sbq = sb("sbq", [P, CT, T])
        sbk = view(vx[:].rearrange("p c t -> p (c t)"), 0, CT, T)
        sbv = view(low, 4 * T, TT, SB)
        xs_flat = xs[:].rearrange("p t d -> p (t d)")
        z_s = view(xs_flat, 0, NZ, W3)
        z_m = view(xs_flat, NZ * W3, NZ, W3)
        sw_pt = view(xs_flat, 0, NZ, W3)
        bonus_v = view(xs_flat, 2 * NZ * W3, TT, C)
        swk = view(krk, NZ * W3, 2, T)
        swv = view(krk, NZ * W3 + 2 * T, TT, SWKV * HD)
        sw_max3 = sb("sw_max3", [P, SWH, 3])
        sw_max = sb("sw_max", [P, 2, SWH])
        sw_neg = sb("sw_neg", [P, 2, SWH])
        sw_es = sb("sw_es", [P, 2, SWH])
        sw_den = sb("sw_den", [P, 2, SWH])

        bank = [ctx.enter_context(nc.psum_tensor(f"bank{i}", [P, BANK], F32)) for i in range(8)]
        GATE_B, UP_B, Y_B = bank[0], bank[1], bank[2:6]
        TR_B = [bank[6], bank[7], bank[0], bank[1]]

        consts = ctx.enter_context(nc.semaphore("consts"))
        ident_ready = ctx.enter_context(nc.semaphore("ident_ready"))
        consts_ready = ctx.enter_context(nc.semaphore("consts_ready"))
        loads_begun = ctx.enter_context(nc.semaphore("loads_begun"))
        x_loaded = ctx.enter_context(nc.semaphore("x_loaded"))
        stored = ctx.enter_context(nc.semaphore("stored"))
        loaded = [Signal(f"loaded{s}", USES[s], step=16) for s in range(SLOTS)]
        hi_ready = [Signal(f"hi_ready{s}", USES[s]) for s in range(SLOTS)]
        split_ready = [Signal(f"split_ready{s}", USES[s], before=1) for s in range(SLOTS)]
        used = [Signal(f"used{s}", USES[s], before=1) for s in range(SLOTS)]
        NPAR = 14
        gain_loaded = Signal("gain_loaded", NORMS, step=16)
        params = Signal("params", NPAR, step=16)
        params_pool = Signal("params_ready", 2)
        HALVES = 2 * TT
        x_ready = Signal("x_ready", NORMS * HALVES, before=HALVES)
        ssq_ready = Signal("ssq_ready", NORMS * HALVES)
        rstd_ready = Signal("rstd_ready", NORMS * TT)
        xs_ready = Signal("xs_ready", NORMS * HALVES, before=1)
        xt_ready = Signal("xt_ready", NORMS * 4)
        act_hi_ready = Signal("act_hi_ready", NORMS * 4)
        act_ready = Signal("act_ready", NORMS * 4)
        silu_ready = Signal("silu_ready", 2 * NG)
        hid_ready = Signal("hid_ready", 2 * NG)
        hid_hi_ready = Signal("hid_hi_ready", 2 * NG)
        hid_split = Signal("hid_split", 2 * NG)
        y_ready = Signal("y_ready", NORMS * 2)
        pool_chain = Chain("pool_chain", 14)
        act_chain = Chain("act_chain", 3)
        dve_chain = Chain("dve_chain", 39)
        proj_out = Signal("proj_out", NIN)
        gate_out = Signal("gate_out", 1)
        zeroed = Signal("zeroed", 6)
        shifted = Signal("shifted", 5)
        mixed = Signal("mixed", 5)
        tw_ready = Signal("tw_ready", 1)
        lora_out = Signal("lora_out", 2)
        sig_ready = Signal("sig_ready", 3)
        sig_g_ready = Signal("sig_g_ready", 1)
        cum_ready = Signal("cum_ready", 2)
        decay_ready = Signal("decay_ready", 3)
        kk_sq_ready = Signal("kk_sq_ready", 1)
        kk_sum = Signal("kk_sum", 1)
        kk_max = Signal("kk_max", 1)
        kk_sqrt = Signal("kk_sqrt", 1)
        chan_ready = Signal("chan_ready", 1)
        bonus_out = Signal("bonus_out", 1)
        bonus_ready = Signal("bonus_ready", 1)
        bonus_v_ready = Signal("bonus_v_ready", 1)
        g_out = Signal("g_out", 1)
        g_ready = Signal("g_ready", 1)
        v_out = Signal("v_out", 1)
        v_ready = Signal("v_ready", 1)
        bk_out = Signal("bk_out", 1)
        bk_ready = Signal("bk_ready", 1)
        pair_out = Signal("pair_out", TT * NH)
        pair_ready = Signal("pair_ready", TT * NH)
        low_out = Signal("low_out", 1)
        inv_ready = Signal("inv_ready", TT * len(LEVELS))
        off_out = Signal("off_out", TT * (len(LEVELS) - 1))
        off_ready = Signal("off_ready", TT * (len(LEVELS) - 1))
        inv_turned = Signal("inv_turned", TT * (len(LEVELS) - 1))
        inv_t_ready = Signal("inv_t_ready", TT * (len(LEVELS) - 1))
        inv_out = Signal("inv_out", TT * (len(LEVELS) - 1))
        rhs_out = Signal("rhs_out", TT)
        rhs_ready = Signal("rhs_ready", TT)
        sa_out = Signal("sa_out", TT)
        sa_ready = Signal("sa_ready", TT)
        s0_out = Signal("s0_out", 1)
        s0_ready = Signal("s0_ready", 1)
        yr_out = Signal("yr_out", TT)
        y_var = Signal("y_var", TT)
        y_rstd_ready = Signal("y_rstd_ready", TT)
        yr_ready = Signal("yr_ready", TT)
        sbz_out = Signal("sbz_out", NH)
        sbz_read = Signal("sbz_read", NH)
        sbl_ready = Signal("sbl_ready", NH // NZ)
        sbm_ready = Signal("sbm_ready", NH)
        sp_ready = Signal("sp_ready", NH)
        sbi_out = Signal("sbi_out", NH)
        arg_ready = Signal("arg_ready", NH)
        sbw_ready = Signal("sbw_ready", NH)
        sbo_out = Signal("sbo_out", NH)
        swk_out = Signal("swk_out", 1)
        swk_swapped = Signal("swk_swapped", 2, step=16)
        swz_out = Signal("swz_out", SWH)
        swz_ready = Signal("swz_ready", SWH)
        sw_max_ready = Signal("sw_max_ready", 1)
        sw_es_ready = Signal("sw_es_ready", 1)
        swe_ready = Signal("swe_ready", SWH)
        swp_ready = Signal("swp_ready", SWH)
        swt_out = Signal("swt_out", SWH)
        swt_ready = Signal("swt_ready", SWH)
        swo_out = Signal("swo_out", SWH)
        TILE_PAIRS = 3
        pair_hi = Signal("pair_hi", TILE_PAIRS)
        pair_split = Signal("pair_split", TILE_PAIRS)
        rwt_out = Signal("rwt_out", TT)
        rwt_hi = Signal("rwt_hi", TT)
        rwt_split = Signal("rwt_split", TT)

        def mix_use(m):
            slot = MIX_SLOT[m]
            return slot, FFN_USES[0][slot] + MIX_SLOT[:m].count(slot)

        def ffn_use(ffn, slot, i):
            return (0 if ffn == 0 else FFN_USES[0][slot] + MIX_USES[slot]) + i

        def down_slot(ffn, i):
            return (ORDER[ffn][0], NG) if isinstance(i, int) and i == NG - 1 else (2, i)

        def up_bank(ffn, i):
            return TR_B[0] if ORDER[ffn][0] == 1 and isinstance(i, int) and i == 0 else UP_B

        def block3(t, n, width):
            return t[:, 0:n * width].rearrange("p (k c) -> p k c", k=n)

        def flat(t):
            return t[:].rearrange("p a b -> p (a b)")

        block = ctx.enter_context(nc.Block())

        @block.sync
        def _(sp):
            def gain_load(layer, norm, w):
                sp.wait_ge(*xs_ready(layer, norm * HALVES))
                sp.sem_inc(loads_begun, 1)
                sp.dma_start(gain[:], w.to_broadcast([P, D])).then_inc(gain_loaded.sem, 16)

            def row(w, layer):
                return w[bass.ds(layer, 1), :]

            def load(layer, slot, use, dst, src):
                sp.wait_ge(*split_ready[slot](layer, use))
                sp.sem_inc(loads_begun, 1)
                sp.dma_start(dst, src).then_inc(loaded[slot].sem, 16)

            def load_in(layer, ffn, w, slot, i):
                src = w.rearrange("l (k p) c -> l p k c", p=P)
                col = slot * F + i * GW
                load(layer, slot, ffn_use(ffn, slot, i), block3(raw[slot], KT, GW),
                     src[layer, :, :, bass.ds(col, GW)])

            def load_down(layer, ffn, w, i):
                src = w.rearrange("l (g k p) c -> l p g k c", k=2, p=P)
                slot, use = down_slot(ffn, i)
                load(layer, slot, ffn_use(ffn, slot, use), block3(raw[slot], 2, D), src[layer, :, i, :, :])

            def ffn_loads(layer, ffn, norm_w, w_in, w_out):
                gain_load(layer, 2 * ffn, row(norm_w, layer))
                load_in(layer, ffn, w_in, ORDER[ffn][0], 0)
                load_in(layer, ffn, w_in, ORDER[ffn][1], 0)
                for slot in ORDER[ffn]:
                    load_in(layer, ffn, w_in, slot, 1)
                load_down(layer, ffn, w_out, 0)
                with sp.Fori(1, NG - 1) as i:
                    for slot in ORDER[ffn]:
                        load_in(layer, ffn, w_in, slot, i + 1)
                    load_down(layer, ffn, w_out, i)
                load_down(layer, ffn, w_out, NG - 1)

            def param_loads(layer):
                def par(dst, src):
                    sp.dma_start(dst, src).then_inc(params.sem, 16)

                rkv = slice(0, 3 * C)
                wa = slice(3 * C, 3 * C + 2 * LORA)
                with nc.allow_non_contiguous_dma(reason="parameters of a few hundred bytes"):
                    par(p_mu[:, 0:6], rw_mu[bass.ds(layer, 1), rkv].rearrange("a (c p) -> p (a c)", p=P))
                    par(p_mu[:, 6:7], rw_mu[bass.ds(layer, 1), wa].rearrange("a p -> p a"))
                    par(p_mug[:], rw_mu[bass.ds(layer, 1), 3 * C + 2 * LORA:]
                        .rearrange("a (c p) -> p (a c)", p=GH))
                    for n, w in enumerate((rw_w0, rw_a0, rw_k_k, rw_k_a)):
                        par(p_vec[:, n, :], row(w, layer).rearrange("a (c p) -> p (a c)", p=P))
                    par(p_vec[:, 4, :], rw_r_k[bass.ds(layer, 1), :, :]
                        .rearrange("a (c h) d -> (h d) (a c)", c=CT))
                par(wa_up[0:LORA, :], rw_w_up[layer, :, :])
                par(wa_up[LORA:P, :], rw_a_up[layer, :, :])
                par(g_up[:], rw_g_up.rearrange("l (j p) c -> l p j c", p=GH)[layer, :, :, :])
                par(gn[:, 0, :], row(rw_gn_g, layer).to_broadcast([P, C]))
                par(gn[:, 1, :], row(rw_gn_b, layer).to_broadcast([P, C]))
                par(sinks[:], row(sw_sinks, layer).to_broadcast([P, SWH]))

            def mixer_loads(layer):
                w_in = mix_w_in.rearrange("l (k p) c -> l p k c", p=P)
                w_out = mix_w_out.rearrange("l (k p) c -> l p k c", p=P)
                for m in range(NMIX):
                    slot, use = mix_use(m)
                    if m < NIN:
                        c0, n = IN_COLS[m]
                        load(layer, slot, use, block3(raw[slot], KT, n), w_in[layer, :, :, c0:c0 + n])
                    else:
                        kt = OUT_KT[m - NIN]
                        load(layer, slot, use, block3(raw[slot], 2, D), w_out[layer, :, kt:kt + 2, :])

            with sp.Fori(0, DEPTH) as layer:
                ffn_loads(layer, 0, ffn1_norm, ffn1_w_in, ffn1_w_out)
                gain_load(layer, 1, row(mix_norm, layer))
                param_loads(layer)
                mixer_loads(layer)
                ffn_loads(layer, 1, ffn2_norm, ffn2_w_in, ffn2_w_out)
            gain_load(DEPTH, 0, final_norm.rearrange("(a d) -> a d", a=1))
            for t in range(TT):
                sp.wait_ge(*xs_ready(DEPTH, 2 * t + 2))
                sp.dma_start(out[0, t * P:(t + 1) * P, :], xs[:, t, :]).then_inc(stored, 16)
            sp.wait_ge(stored, 16 * TT)

        @block.gpsimd
        def _(pool):
            n_const = [0]

            def const(instruction):
                n_const[0] += 1
                instruction.then_inc(consts, 1)
                pool.wait_ge(consts, n_const[0])

            def keep(t, pattern, base, channel, fill=0.0):
                const(pool.affine_select(t, t, pattern, ALU.is_ge, fill, base, channel))

            def rstd_of(layer, norm, chained_at=None):
                for t in range(TT):
                    ms = meansq[:, t:t + 1]
                    for half, other in ((0, eps[:, 0:1]), (1, ms)):
                        pool.wait_ge(*ssq_ready(layer, norm * HALVES + 2 * t + half + 1))
                        pool_chain.link(pool, layer if chained_at is None else chained_at,
                                        pool.tensor_tensor(ms, ssq[:, t, half:half + 1], other, ALU.add))
                    pool.tensor_tensor(rstd[:, t:t + 1], ms, minus_half[:, 0:1], ALU.pow) \
                        .then_inc(rstd_ready.sem, 1)


            const(pool.memset(eps[:], NORM_EPS))
            const(pool.memset(minus_half[:], -0.5))
            const(pool.memset(ident[:], 1.0))
            keep(ident[:], [[1, P]], 0, -1)
            pool.affine_select(ident[:], ident[:], [[-1, P]], ALU.is_ge, 0.0, 0, 1) \
                .then_inc(ident_ready, 1)
            pool.wait_ge(ident_ready, 1)
            rstd_of(0, 0)
            const(pool.memset(ones[:], 1.0))
            for t in (suffix, head_ones):
                const(pool.tensor_copy(t[:], ones[:]))
            keep(suffix[:], [[-1, P]], 0, 1)
            keep(head_ones[:], [[-HD, 2], [0, HD]], 0, 1)
            keep(head_ones[:], [[HD, 2], [0, HD]], HD - 1, -1)
            const(pool.tensor_copy(head_of[:], head_ones[:].rearrange("p (h d) -> p h d", h=2)[:, :, 0]))
            const(pool.memset(before[:], 1.0))
            const(pool.memset(not_before[:], 0.0))
            for lo in (0, 2 * P):
                keep(before[:, lo:lo + P], [[1, P]], -1, -1)
                keep(not_before[:, lo:lo + P], [[1, P]], -1, -1, -FAR)
            const(pool.memset(pair_mask[:], 1.0))
            keep(pair_mask[:, :, 0, :], [[0, 2], [1, P]], -1, -1)
            keep(pair_mask[:, :, 1, :], [[0, 2], [1, P]], 0, -1)
            const(pool.memset(level_mask[:], 0.0))
            for i, n in enumerate(LEVELS):
                first = level_mask[:, i, :].rearrange("p (b r u) -> p b r u", r=2, u=n)[:, :, 0, :]
                const(pool.memset(first, 1.0))
                keep(first, [[-2 * n, P // (2 * n)], [0, n]], -n, 1)
                keep(first, [[2 * n, P // (2 * n)], [0, n]], 2 * n - 1, -1)
            const(pool.iota(dist[:, 0:P], [[-1, P]], 0, 1, allow_small_or_imprecise_dtypes=True))
            const(pool.iota(dist[:, P:], [[-1, 2 * P]], P, 1, allow_small_or_imprecise_dtypes=True))
            keep(dist[:, 0:P], [[-1, P]], 0, 1, FAR)
            keep(dist[:, P:], [[-1, 2 * P]], P, 1, FAR)
            keep(dist[:, P:], [[1, 2 * P]], WINDOW - 1 - P, -1, FAR)
            const(pool.memset(s0[:], 0.0))
            pool.memset(gn_eps[:], GN_EPS).then_inc(consts_ready, 1)
            pool.wait_ge(consts_ready, 1)


            def mixer(layer):
                for n, t in enumerate((lora_p[:, 0:1], gate_p[:, :, 0:1], k_p[:, :, 0:1], r_p[:, :, 0:1],
                                       v_p[:, :, 0:1], cum[:, :, 0:1])):
                    pool.memset(t, 0.0).then_inc(zeroed.sem, 1)
                pool.wait_ge(*zeroed(layer, 6))

                def diff(d, src):
                    pool.tensor_tensor(d, src[..., 0:T], src[..., 1:T + 1], ALU.subtract) \
                        .then_inc(shifted.sem, 1)

                pool.wait_ge(*proj_out(layer, 1))
                diff(xwa, lora_p)
                pool.wait_ge(*gate_out(layer, 1))
                diff(xg, gate_p)
                for m, d, src in ((1, kx, k_p), (2, rx, r_p), (3, vx, v_p)):
                    pool.wait_ge(*proj_out(layer, m + 1))
                    diff(d[:], src)
                for h in range(NH):
                    pool.wait_ge(*sbz_read(layer, h + 1))
                    if h >= NZ:
                        pool.wait_ge(*arg_ready(layer, h + 1 - NZ))
                    pool.tensor_tensor(z_m[:, h % NZ, :], z_s[:, h % NZ, :], not_before[:], ALU.add) \
                        .then_inc(sbm_ready.sem, 1)
                pool.wait_ge(*bonus_ready(layer, 1))
                pool.wait_ge(*v_ready(layer, 1))
                pool.tensor_tensor(
                    bonus_v[:].rearrange("p q (h d) -> p (q h) d", h=NH),
                    v_tok[:].rearrange("p q (h d) -> p (q h) d", h=NH),
                    bonus[:].rearrange("p q h -> p (q h)").unsqueeze(2).to_broadcast([P, TT * NH, HD]),
                    ALU.mult).then_inc(bonus_v_ready.sem, 1)
                for q in range(TT):
                    pool.wait_ge(*y_var(layer, q + 1))
                    pool_chain.link(pool, layer, pool.tensor_tensor(
                        y_rstd[:, q, :], y_rstd[:, q, :], gn_eps[:, 0:NH], ALU.add))
                    pool.tensor_tensor(y_rstd[:, q, :], y_rstd[:, q, :], minus_half[:, 0:NH], ALU.pow) \
                        .then_inc(y_rstd_ready.sem, 1)

            with pool.Fori(0, DEPTH) as layer:
                rstd_of(layer, 1)
                mixer(layer)
                rstd_of(layer, 2)
                rstd_of(layer + 1, 0, chained_at=layer)
            pool_chain.ended(ahead=2 * TT)

        @block.scalar
        def _(act):
            def hi(layer, slot, use, n):
                act.wait_ge(*loaded[slot](layer, use + 1))
                act.wait_ge(*used[slot](layer, use))
                act.copy(w_hi[slot][:, 0:n], raw[slot][:, 0:n]).then_inc(hi_ready[slot].sem, 1)

            def ffn_hi(layer, ffn, slot, i):
                hi(layer, slot, ffn_use(ffn, slot, i), KT * GW)

            def down_hi(layer, ffn, i):
                slot, use = down_slot(ffn, i)
                ffn_hi(layer, ffn, slot, use)

            def mix_hi(layer, m):
                slot, use = mix_use(m)
                hi(layer, slot, use, KT * IN_COLS[m][1] if m < NIN else 2 * D)

            def norm_squares(layer, norm, t):
                for half in range(2):
                    cols = slice(half * BANK, (half + 1) * BANK)
                    act.wait_ge(*x_ready(layer, (norm - 1) * HALVES + 2 * t + half + 1))
                    act.activation(xs[:, t, cols], x_sb[:, t, cols], ACT.Square, scale=D ** -0.5,
                                   accum_out=ssq[:, t, half:half + 1]).then_inc(ssq_ready.sem, 1)

            def norm_hi(layer, norm, t):
                for b in range(2):
                    act.wait_ge(*xt_ready(layer, norm * 4 + 2 * t + b + 1))
                    act.copy(act_hi[:, 4 * b:4 * b + 4, t * P:(t + 1) * P],
                             TR_B[2 * t + b][:].rearrange("p (k t) -> p k t", k=4)).then_inc(act_hi_ready.sem, 1)

            def ffn(layer, ffn):
                def gate(i):
                    n = ffn * NG + i
                    act.wait_ge(*used[0](layer, ffn_use(ffn, 0, i) + 1))
                    if not isinstance(i, int) or i > 0:
                        act.wait_ge(*hid_ready(layer, n))
                    act.activation(silu[:], GATE_B[:], ACT.Silu).then_inc(silu_ready.sem, 1)

                def gate_and_next(i):
                    for slot in ORDER[ffn]:
                        if slot == 0:
                            gate(i)
                        if slot == ORDER[ffn][0]:
                            ffn_hi(layer, ffn, slot, i + 1)
                    ffn_hi(layer, ffn, ORDER[ffn][1], i + 1)

                gate_and_next(0)
                with act.Fori(1, NG - 1) as i:
                    down_hi(layer, ffn, i - 1)
                    gate_and_next(i)
                down_hi(layer, ffn, NG - 2)
                if ORDER[ffn][0] == 0:
                    gate(NG - 1)
                down_hi(layer, ffn, NG - 1)
                if ORDER[ffn][0] == 1:
                    gate(NG - 1)

            def piece_out(layer, m):
                slot, use = mix_use(m)
                act.wait_ge(*used[slot](layer, use + 1))

            def mixer(layer):
                def project_out(m, dst, src, scale=1.0):
                    piece_out(layer, m)
                    act.activation(dst, src, ACT.Copy, scale=scale).then_inc(proj_out.sem, 1)
                    if m + SLOTS < NIN + 1:
                        mix_hi(layer, m + SLOTS)

                def two(b):
                    return bank[b][:].rearrange("p (c t) -> p c t", c=2)

                piece_out(layer, 0)
                act.copy(gate_p[:, :, 1:], bank[2][0:GH, :].rearrange("p (c t) -> p c t", c=2)) \
                    .then_inc(gate_out.sem, 1)
                project_out(0, lora_p[:, 1:], bank[0][:, 0:T])
                project_out(1, k_p[:, :, 1:], two(1))
                act.wait_ge(*mixed(layer, 1))
                act.activation(tw[:], xwa[0:LORA, :], ACT.Tanh).then_inc(tw_ready.sem, 1)
                act.wait_ge(*mixed(layer, 2))
                act.activation(sig_g[:], xg[:], ACT.Tanh, scale=0.5).then_inc(sig_ready.sem, 1)
                project_out(2, r_p[:, :, 1:], two(0))
                act.wait_ge(*params_pool(layer, 2))
                for n, s in ((0, sig_w), (1, sig_a)):
                    act.wait_ge(*lora_out(layer, n + 1))
                    for c in range(CT):
                        ins = act.activation(s[:, c, :], bank[3 + n][:, c * T:(c + 1) * T], ACT.Tanh,
                                             bias=p_half[:, n, c:c + 1], scale=0.5)
                    ins.then_inc(sig_ready.sem, 1)
                project_out(3, v_p[:, :, 1:], two(1))
                act.wait_ge(*kk_max(layer, 1))
                act.activation(kk_norm[:], kk_norm[:], ACT.Sqrt).then_inc(kk_sqrt.sem, 1)
                project_out(4, sbq[:], two(0), SCALE)
                act.wait_ge(*cum_ready(layer, 2))
                act.activation(pos[:], cumc[:], ACT.Exp, scale=-1.0).then_inc(decay_ready.sem, 1)
                act.activation(neg[:], cumc[:, :, 1:], ACT.Exp).then_inc(decay_ready.sem, 1)
                act.activation(hop_decay[:], hop[:], ACT.Exp, scale=-1.0).then_inc(decay_ready.sem, 1)
                act.wait_ge(*v_out(layer, 1))
                act.copy(v_tok[:], two(5)).then_inc(v_ready.sem, 1)
                project_out(5, sbk[:], two(1))
                project_out(6, sbv[:], two(0))
                act.wait_ge(*g_out(layer, 1))
                act.copy(g_tok[:], two(2)).then_inc(g_ready.sem, 1)
                project_out(7, swq[:, 0:2, :], two(1), SCALE)
                act.wait_ge(*bk_out(layer, 1))
                act.copy(bk_tok[:], two(3)).then_inc(bk_ready.sem, 1)
                project_out(8, swq[:, 2:4, :], two(0), SCALE)

                def sb_log(pair):
                    if pair:
                        last = pair * NZ
                        act.wait_ge(*sp_ready(layer, last))
                        act.wait_ge(*sbm_ready(layer, last))
                        act.wait_ge(*sbw_ready(layer, last))
                    for i in range(NZ):
                        z = bank[6 + i][:, 0:3 * P]
                        act.wait_ge(*sbz_out(layer, pair * NZ + i + 1))
                        act.copy(z_s[:, i, :], z)
                        act.activation(z_e[:, i, :], z, ACT.Abs).then_inc(sbz_read.sem, 1)
                    act.wait_ge(*sbz_read(layer, pair * NZ + NZ))
                    act_chain.link(act, layer, act.activation(z_e[:], z_e[:], ACT.Exp, scale=-1.0))
                    act.activation(z_l[:], z_e[:], ACT.Ln, bias=1.0).then_inc(sbl_ready.sem, 1)

                sb_log(0)
                act.wait_ge(*swk_out(layer, 1))
                act_chain.link(act, layer, act.copy(swk[:, 0, :], bank[1][:, 0:T]))
                for half in range(2):
                    act.dma_start(swk[half * HD:(half + 1) * HD, 1, :],
                                  swk[(1 - half) * HD:(2 - half) * HD, 0, :]).then_inc(swk_swapped.sem, 16)

                def sb_exp(h):
                    i = h % NZ
                    act.wait_ge(*arg_ready(layer, h + 1))
                    act.activation(sb_w[:, i, :], z_e[:, i, :], ACT.Exp).then_inc(sbw_ready.sem, 1)

                def tiles_hi(pair, k0, n_out, signal):
                    act.wait_ge(*signal(layer, n_out))
                    act.copy(act_hi[:, k0:k0 + 2, :], two(pair % 2)).then_inc(pair_hi.sem, 1)

                def sw_sink():
                    act.wait_ge(*sw_max_ready(layer, 1))
                    act.activation(sw_es[:], sw_es[:], ACT.Exp).then_inc(sw_es_ready.sem, 1)

                def sw_exp(h):
                    for t, lo, hi_ in ((0, 0, P), (1, P, 3 * P)):
                        ins = act.activation(sw_p[:, h, lo:hi_], sw_p[:, h, lo:hi_], ACT.Exp,
                                             bias=sw_neg[:, t, h:h + 1], accum_out=sw_den[:, t, h:h + 1])
                    ins.then_inc(swe_ready.sem, 1)

                def sw_turn(h):
                    i = h % NZ
                    act.wait_ge(*swt_out(layer, h + 1))
                    if h >= NZ:
                        act.wait_ge(*swo_out(layer, h + 1 - NZ))
                    act.copy(sw_pt[:, i, :], bank[6 + i][:, 0:3 * P]).then_inc(swt_ready.sem, 1)

                for slot in range(NSLOT):
                    lev, phase = slot // 2 + 1, slot % 2
                    if phase == 0:
                        for q in range(TT):
                            act.wait_ge(*inv_turned(layer, (lev - 1) * TT + q + 1))
                            act.copy(inv_t[:, q * NH:(q + 1) * NH, :],
                                     bank[4 + q][:].rearrange("p (h t) -> p h t", h=NH)) \
                                .then_inc(inv_t_ready.sem, 1)
                    for what, h in SLOT[slot]:
                        if what == "hi":
                            mix_hi(layer, h)
                        elif what == "v" and h == TT - 1:
                            project_out(9, swv[:], bank[1][:, T:].rearrange("p (c t) -> p c t", c=TT))
                        elif what == "sbz":
                            if h % NZ == 0:
                                sb_log(h // NZ)
                        elif what == "sbi":
                            sb_exp(h)
                        elif what == "sbout":
                            tiles_hi(0, 0, NH, sbo_out)
                        elif what == "swmax":
                            sw_sink()
                        elif what == "swe":
                            sw_exp(h)
                        elif what == "swt":
                            sw_turn(h)
                        elif what == "swout":
                            tiles_hi(1 + h, 4 + 2 * h, 4 * (h + 1), swo_out)

                def sa_copy(q):
                    act.wait_ge(*sa_out(layer, q + 1))
                    act.copy(sa[:, q, :], bank[7][:, 0:C]).then_inc(sa_ready.sem, 1)

                def heads_hi(q):
                    act.wait_ge(*rwt_out(layer, q + 1))
                    act.copy(act_hi[:, 2:4, q * P:(q + 1) * P],
                             bank[6 + q][:, 0:2 * P].rearrange("p (c t) -> p c t", c=CT)) \
                        .then_inc(rwt_hi.sem, 1)

                sa_copy(0)
                sa_copy(1)
                mix_hi(layer, 13)
                heads_hi(0)
                ffn_hi(layer, 1, ORDER[1][0], 0)
                heads_hi(1)

            for t in range(TT):
                act.dma_start(x_sb[:, t, :], x[0, t * P:(t + 1) * P, :]).then_inc(x_loaded, 16)
            for t in range(TT):
                norm_squares(0, 0, t)
            with act.Fori(0, DEPTH) as layer:
                norm_hi(layer, 0, 0)
                ffn_hi(layer, 0, ORDER[0][0], 0)
                norm_hi(layer, 0, 1)
                ffn_hi(layer, 0, ORDER[0][1], 0)
                ffn(layer, 0)
                mix_hi(layer, 0)
                for t in range(TT):
                    norm_squares(layer, 1, t)
                for t in range(TT):
                    norm_hi(layer, 1, t)
                mix_hi(layer, 1)
                mix_hi(layer, 2)
                mixer(layer)
                for t in range(TT):
                    norm_squares(layer, 2, t)
                for t in range(TT):
                    norm_hi(layer, 2, t)
                ffn_hi(layer, 1, ORDER[1][1], 0)
                ffn(layer, 1)
                for t in range(TT):
                    norm_squares(layer + 1, 0, t)
            act_chain.ended()

        @block.vector
        def _(dve):
            def lo(layer, slot, use, n):
                dve.wait_ge(*hi_ready[slot](layer, use + 1))
                dve.tensor_tensor(w_lo[slot][:, 0:n], raw[slot][:, 0:n],
                                  w_hi[slot][:, 0:n].bitcast(F32), ALU.subtract) \
                    .then_inc(split_ready[slot].sem, 1)

            def ffn_lo(layer, ffn, slot, i):
                lo(layer, slot, ffn_use(ffn, slot, i), KT * GW)

            def down_lo(layer, ffn, i):
                slot, use = down_slot(ffn, i)
                ffn_lo(layer, ffn, slot, use)

            def mix_lo(layer, m):
                slot, use = mix_use(m)
                lo(layer, slot, use, KT * IN_COLS[m][1] if m < NIN else 2 * D)

            def norm_scale(layer, norm, t):
                dve.wait_ge(*gain_loaded(layer, norm + 1))
                dve.wait_ge(*rstd_ready(layer, norm * TT + t + 1))
                for half in range(2):
                    cols = slice(half * BANK, (half + 1) * BANK)
                    dve.scalar_tensor_tensor(xs[:, t, cols], x_sb[:, t, cols], rstd[:, t:t + 1], gain[:, cols],
                                             ALU.mult, ALU.mult).then_inc(xs_ready.sem, 1)

            def norm_lo(layer, norm, t):
                for b in range(2):
                    dst = (slice(None), slice(4 * b, 4 * b + 4), slice(t * P, (t + 1) * P))
                    dve.wait_ge(*act_hi_ready(layer, norm * 4 + 2 * t + b + 1))
                    dve.tensor_tensor(act_lo[dst], TR_B[2 * t + b][:].rearrange("p (k t) -> p k t", k=4),
                                      act_hi[dst].bitcast(F32), ALU.subtract).then_inc(act_ready.sem, 1)

            def residual(layer, norm, t):
                slot, use = mix_use(NMIX - 1) if norm == 1 else \
                    (ORDER[norm // 2][0], ffn_use(norm // 2, ORDER[norm // 2][0], NG))
                for half in range(2):
                    if t == 1 and half == 1:
                        dve.wait_ge(*used[slot](layer, use + 1))
                    elif half == 0:
                        dve.wait_ge(*y_ready(layer, 2 * norm + t + 1))
                    cols = slice(half * BANK, (half + 1) * BANK)
                    dve.scalar_tensor_tensor(x_sb[:, t, cols], Y_B[2 * t + half][:],
                                                   1.0 if norm == 1 else 0.5, x_sb[:, t, cols],
                                                   ALU.mult, ALU.add).then_inc(x_ready.sem, 1)

            def ffn(layer, ffn):
                def hidden(i):
                    n = ffn * NG + i
                    dve.wait_ge(*silu_ready(layer, n + 1))
                    dve.wait_ge(*used[1](layer, ffn_use(ffn, 1, i) + 1))
                    if not isinstance(i, int) or i > 0:
                        dve.wait_ge(*hid_split(layer, n))
                    dve.tensor_tensor(hid[:], up_bank(ffn, i)[:], silu[:], ALU.mult).then_inc(hid_ready.sem, 1)

                def hidden_split(i):
                    n = ffn * NG + i
                    own = isinstance(i, int) and i == NG - 1
                    h, l = (last_hi, last_lo) if own else (hid_hi[:], hid_lo[:])
                    whole = hid[:].rearrange("p (a b) -> p a b", a=2 * TT if own else 2)
                    dve.wait_ge(*hid_ready(layer, n + 1))
                    if not own:
                        dve.wait_ge(*used[2](layer, ffn_use(ffn, 2, i)))
                    dve.tensor_copy(h, whole).then_inc(hid_hi_ready.sem, 1)
                    dve.wait_ge(*hid_hi_ready(layer, n + 1))
                    dve.tensor_tensor(l, whole, h.bitcast(F32), ALU.subtract) \
                        .then_inc(hid_split.sem, 1)

                first, second = ORDER[ffn]
                ffn_lo(layer, ffn, first, 1)
                hidden(0)
                ffn_lo(layer, ffn, second, 1)
                with dve.Fori(1, NG - 1) as i:
                    hidden_split(i - 1)
                    down_lo(layer, ffn, i - 1)
                    ffn_lo(layer, ffn, first, i + 1)
                    hidden(i)
                    ffn_lo(layer, ffn, second, i + 1)
                hidden_split(NG - 2)
                down_lo(layer, ffn, NG - 2)
                down_lo(layer, ffn, NG - 1)
                hidden(NG - 1)
                hidden_split(NG - 1)

            def mixer(layer):
                def link(ins):
                    dve_chain.link(dve, layer, ins)

                def shift(n, dst, src, mu):
                    dve.wait_ge(*shifted(layer, n))
                    for c, m in enumerate(mu):
                        at = (slice(None), c) if len(mu) > 1 else (slice(None),)
                        cur = src[:, c, 1:] if len(mu) > 1 else src[:, 1:]
                        ins = dve.scalar_tensor_tensor(dst[at], dst[at], m, cur, ALU.mult, ALU.add)
                    ins.then_inc(mixed.sem, 1)
                    dve.wait_ge(*mixed(layer, n))

                def chan(n, c):
                    return p_vec[:, n, c:c + 1]

                mix_lo(layer, 3)
                shift(1, xwa, lora_p, [p_mu[:, 6:7]])
                shift(2, xg, gate_p, [p_mug[:, 0:1], p_mug[:, 1:2]])
                mix_lo(layer, 4)
                shift(3, kx, k_p, [p_mu[:, 2:3], p_mu[:, 3:4]])
                for c in range(CT):
                    ins = dve.tensor_scalar(kkr[:, c, :], kx[:, c, :], chan(2, c), None, ALU.mult)
                link(ins)
                dve.tensor_tensor(kk_sq[:], kkr[:], kkr[:], ALU.mult).then_inc(kk_sq_ready.sem, 1)
                dve.wait_ge(*sig_ready(layer, 1))
                dve.tensor_scalar(sig_g[:], sig_g[:], 0.5, 0.5, ALU.mult, ALU.add) \
                    .then_inc(sig_g_ready.sem, 1)
                mix_lo(layer, 5)
                shift(4, rx, r_p, [p_mu[:, 0:1], p_mu[:, 1:2]])
                dve.wait_ge(*sig_ready(layer, 2))
                link(dve.tensor_scalar(sig_w[:], sig_w[:], 0.5 * E05, 0.5 * E05, ALU.mult, ALU.add))
                for c in range(CT):
                    for q in range(TT):
                        ins = dve.tensor_tensor_scan(cum[:, c * TT + q, 1:], ones[:],
                                                     sig_w[:, c, q * P:(q + 1) * P], 0.0, ALU.mult, ALU.add)
                ins.then_inc(cum_ready.sem, 1)
                dve.wait_ge(*cum_ready(layer, 1))
                link(dve.tensor_tensor(cumc[:], cum[:], cum[:, :, P // 2:P // 2 + 1]
                                       .to_broadcast([P, CT * TT, P + 1]), ALU.subtract))
                dve.tensor_tensor(hop[:], cumc[:, 0::TT, P], cum[:, 1::TT, P // 2], ALU.add) \
                    .then_inc(cum_ready.sem, 1)
                dve.wait_ge(*kk_sum(layer, 1))
                dve.tensor_scalar(kk_norm[:], bank[5][:], 1e-24, None, ALU.max).then_inc(kk_max.sem, 1)
                dve.wait_ge(*sig_ready(layer, 3))
                link(dve.tensor_scalar(sig_a[:], sig_a[:], 0.5, 0.5, ALU.mult, ALU.add))
                mix_lo(layer, 6)
                for c in range(CT):
                    ins = dve.tensor_scalar(kd[:, c, :], sig_a[:, c, :], chan(3, c), p_1mka[:, c:c + 1],
                                            ALU.mult, ALU.add)
                link(ins)
                link(dve.tensor_tensor(kd[:], kd[:], kx[:], ALU.mult))
                shift(5, vx, v_p, [p_mu[:, 4:5], p_mu[:, 5:6]])
                mix_lo(layer, 7)
                dve.wait_ge(*kk_sqrt(layer, 1))
                link(dve.reciprocal(kk_norm[:], kk_norm[:]))
                link(dve.tensor_tensor(flat(kk), flat(kkr), kk_norm[:], ALU.mult))
                link(dve.tensor_tensor(kkr[:], kk[:], sig_a[:], ALU.mult))

                def chunks(t):
                    return t[:].rearrange("p c (q t) -> p (c q) t", q=TT)

                for c in range(CT):
                    dve.scalar_tensor_tensor(rkk[:, c, :], rx[:, c, :], chan(4, c), kd[:, c, :],
                                             ALU.mult, ALU.mult)
                dve.wait_ge(*decay_ready(layer, 2))
                dve.tensor_tensor(ar[:, :, 0, :], chunks(kk), pos[:, :, 0:P], ALU.mult)
                dve.tensor_tensor(ar[:, :, 1, :], chunks(rx), pos[:, :, 1:], ALU.mult)
                dve.tensor_tensor(bm[:], chunks(kkr), neg[:], ALU.mult)
                dve.tensor_tensor(km[:], chunks(kd), neg[:], ALU.mult).then_inc(chan_ready.sem, 1)
                mix_lo(layer, 8)
                mix_lo(layer, 9)
                dve.wait_ge(*bonus_out(layer, 1))
                dve.tensor_copy(bonus[:], bank[4][:, 0:TT * NH].rearrange("p (q h) -> p q h", q=TT)) \
                    .then_inc(bonus_ready.sem, 1)
                mix_lo(layer, 10)

                def mat4(q):
                    return slice(q * NH, (q + 1) * NH)

                def four(b):
                    return b[:].rearrange("p (h t) -> p h t", h=NH)

                def over4(m):
                    return m.unsqueeze(1).to_broadcast([P, NH, P])

                for n in range(TT * NH):
                    dve.wait_ge(*pair_out(layer, n + 1))
                    dve.tensor_tensor(pm[:, n, :, :].rearrange("p a t -> p (a t)"), bank[2 + n % 2][:],
                                      pair_mask[:].rearrange("p a b t -> p (a b t)"), ALU.mult) \
                        .then_inc(pair_ready.sem, 1)
                dve.wait_ge(*low_out(layer, 1))
                for b in range(2):
                    link(dve.tensor_tensor(inv[:, b::2, :], four(bank[4 + b]), over4(level_mask[:, 0, :]),
                                           ALU.mult))
                for q in range(TT):
                    dve.tensor_tensor(inv[:, mat4(q), :], over4(ident[:]), inv[:, mat4(q), :],
                                      ALU.subtract).then_inc(inv_ready.sem, 1)

                def sp_plus(h):
                    i = h % NZ
                    dve.wait_ge(*sbl_ready(layer, h // NZ + 1))
                    link(dve.scalar_tensor_tensor(z_l[:, i, :], z_s[:, i, :], 0.0, z_l[:, i, :],
                                                  ALU.max, ALU.add))
                    dve.tensor_tensor(sp_m[:, i, :], z_l[:, i, :], before[:], ALU.mult) \
                        .then_inc(sp_ready.sem, 1)

                def sb_arg(h):
                    i = h % NZ
                    dve.wait_ge(*sbi_out(layer, h + 1))
                    dve.wait_ge(*sbm_ready(layer, h + 1))
                    dve.tensor_tensor(z_e[:, i, :], z_m[:, i, :], bank[6 + i][:, 0:3 * P], ALU.subtract) \
                        .then_inc(arg_ready.sem, 1)

                def tiles_lo(pair, k0):
                    dve.wait_ge(*pair_hi(layer, pair + 1))
                    dve.tensor_tensor(act_lo[:, k0:k0 + 2, :], bank[pair % 2][:].rearrange("p (c t) -> p c t", c=2),
                                      act_hi[:, k0:k0 + 2, :].bitcast(F32), ALU.subtract) \
                        .then_inc(pair_split.sem, 1)

                def sw_bias(h):
                    slope = 2.0 ** (-8.0 * (h + 1) / SWH)
                    dve.wait_ge(*swz_out(layer, h + 1))
                    if h == 0:
                        dve.wait_ge(*sbw_ready(layer, NH))
                    dve.scalar_tensor_tensor(sw_p[:, h, :], dist[:], -slope, bank[6 + h % NZ][:, 0:3 * P],
                                             ALU.mult, ALU.add).then_inc(swz_ready.sem, 1)
                    dve.wait_ge(*swz_ready(layer, h + 1))
                    ins = dve.tensor_reduce(sw_max3[:, h, :], sw_p[:, h, :].rearrange("p (b s) -> p b s", b=3),
                                            AX_X, ALU.max)
                    if h == SWH - 1:
                        link(ins)

                def sw_maxima():
                    link(dve.tensor_tensor(sw_max[:, 0, :], sw_max3[:, :, 0], sinks[:], ALU.max))
                    link(dve.tensor_tensor(sw_max[:, 1, :], sw_max3[:, :, 1], sw_max3[:, :, 2], ALU.max))
                    link(dve.tensor_tensor(sw_max[:, 1, :], sw_max[:, 1, :], sinks[:], ALU.max))
                    dve.tensor_scalar(sw_neg[:], sw_max[:], -1.0, None, ALU.mult)
                    dve.tensor_tensor(sw_es[:], sinks[:].unsqueeze(1).to_broadcast([P, 2, SWH]), sw_max[:],
                                      ALU.subtract).then_inc(sw_max_ready.sem, 1)

                def sw_norm(half):
                    hs = slice(4 * half, 4 * half + 4)
                    dve.wait_ge(*swe_ready(layer, 4 * half + 4))
                    dve.wait_ge(*sw_es_ready(layer, 1))
                    link(dve.tensor_tensor(sw_den[:, :, hs], sw_den[:, :, hs], sw_es[:, :, hs], ALU.add))
                    link(dve.reciprocal(sw_den[:, :, hs], sw_den[:, :, hs]))
                    for h in range(4 * half, 4 * half + 4):
                        for t, a, b in ((0, 0, P), (1, P, 3 * P)):
                            ins = dve.tensor_scalar(sw_p[:, h, a:b], sw_p[:, h, a:b], sw_den[:, t, h:h + 1],
                                                    None, ALU.mult)
                        ins.then_inc(swp_ready.sem, 1)

                for h in range(NZ):
                    sp_plus(h)
                for slot in range(NSLOT):
                    lev, phase = slot // 2 + 1, slot % 2
                    for q in range(TT):
                        if slot // 2 >= len(LEVELS) - 1:
                            break
                        n = (lev - 1) * TT + q + 1
                        if phase == 0:
                            dve.wait_ge(*off_out(layer, n))
                            dve.tensor_tensor(off[:, mat4(q), :], four(bank[2 + q]),
                                              over4(level_mask[:, lev, :]), ALU.mult) \
                                .then_inc(off_ready.sem, 1)
                        else:
                            dve.wait_ge(*inv_out(layer, n))
                            t, b = (inv, bank[4 + q]) if lev < len(LEVELS) - 1 else (inv_t, bank[2 + q])
                            dve.tensor_tensor(t[:, mat4(q), :], t[:, mat4(q), :], four(b), ALU.subtract) \
                                .then_inc(inv_ready.sem, 1)
                    for what, h in SLOT[slot]:
                        if what == "lo":
                            mix_lo(layer, h)
                        elif what == "sbz":
                            sp_plus(h)
                        elif what == "sbi":
                            sb_arg(h)
                        elif what == "sbout":
                            tiles_lo(0, 0)
                        elif what == "swz":
                            sw_bias(h)
                        elif what == "swmax":
                            sw_maxima()
                        elif what == "swn":
                            sw_norm(h)
                        elif what == "swout":
                            tiles_lo(1 + h, 4 + 2 * h)

                def negate_rhs(q):
                    dve.wait_ge(*rhs_out(layer, q + 1))
                    dve.tensor_scalar(rhs[:, q, :], bank[6][:, 0:C], -1.0, None, ALU.mult) \
                        .then_inc(rhs_ready.sem, 1)

                def heads(t, q):
                    return t[:, q, :].rearrange("p (h d) -> p h d", h=NH)

                def per_head(t, q):
                    return t[:, q, :].unsqueeze(2).to_broadcast([P, NH, HD])

                def group_norm(q):
                    y = bank[q][:, 0:C].rearrange("p (h d) -> p h d", h=NH)
                    dve.wait_ge(*yr_out(layer, q + 1))
                    link(dve.tensor_reduce(y_sum[:, q, :], y, AX_X, ALU.add))
                    link(dve.tensor_scalar(y_sum[:, q, :], y_sum[:, q, :], -1.0 / HD, None, ALU.mult))
                    link(dve.tensor_tensor(heads(y_c, q), y, per_head(y_sum, q), ALU.add))
                    link(dve.scalar_tensor_tensor(y_sq[:, q, :], y_c[:, q, :], 1.0 / HD, y_c[:, q, :],
                                                  ALU.mult, ALU.mult))
                    dve.tensor_reduce(y_rstd[:, q, :], heads(y_sq, q), AX_X, ALU.add) \
                        .then_inc(y_var.sem, 1)

                def gate_heads(q):
                    dve.wait_ge(*y_rstd_ready(layer, q + 1))
                    link(dve.tensor_tensor(heads(y_c, q), heads(y_c, q), per_head(y_rstd, q), ALU.mult))
                    link(dve.tensor_tensor(y_c[:, q, :], y_c[:, q, :], gn[:, 0, :], ALU.mult))
                    link(dve.tensor_tensor(y_c[:, q, :], y_c[:, q, :], gn[:, 1, :], ALU.add))
                    dve.wait_ge(*bonus_v_ready(layer, 1))
                    link(dve.tensor_tensor(y_c[:, q, :], y_c[:, q, :], bonus_v[:, q, :], ALU.add))
                    dve.wait_ge(*g_ready(layer, 1))
                    dve.tensor_tensor(y_c[:, q, :], y_c[:, q, :], g_tok[:, q, :], ALU.mult) \
                        .then_inc(yr_ready.sem, 1)

                negate_rhs(0)
                dve.wait_ge(*s0_out(layer, 1))
                dve.wait_ge(*decay_ready(layer, 3))
                for h in range(NH):
                    c, ch = h // 2, slice(HD * (h % 2), HD * (h % 2) + HD)
                    ins = dve.tensor_scalar(s0[ch, c, h % 2, :],
                                            bank[1][ch, BANK - C + c * HD:BANK - C + (c + 1) * HD],
                                            hop_decay[ch, c:c + 1], None, ALU.mult)
                ins.then_inc(s0_ready.sem, 1)

                def heads_lo(q):
                    dve.wait_ge(*rwt_hi(layer, q + 1))
                    dst = (slice(None), slice(2, 4), slice(q * P, (q + 1) * P))
                    dve.tensor_tensor(act_lo[dst], bank[6 + q][:, 0:2 * P].rearrange("p (c t) -> p c t", c=CT),
                                      act_hi[dst].bitcast(F32), ALU.subtract).then_inc(rwt_split.sem, 1)

                negate_rhs(1)
                group_norm(0)
                gate_heads(0)
                group_norm(1)
                mix_lo(layer, 13)
                heads_lo(0)
                gate_heads(1)
                ffn_lo(layer, 1, ORDER[1][0], 0)
                heads_lo(1)

            for s in range(SLOTS):
                dve.engine_nop().then_inc(split_ready[s].sem, 1)
                dve.engine_nop().then_inc(used[s].sem, 1)
            dve.engine_nop().then_inc(xs_ready.sem, 1)
            dve.wait_ge(x_loaded, 16 * TT)
            for _ in range(HALVES):
                dve.engine_nop().then_inc(x_ready.sem, 1)
            norm_scale(0, 0, 0)
            with dve.Fori(0, DEPTH) as layer:
                norm_scale(layer, 0, 1)
                norm_lo(layer, 0, 0)
                ffn_lo(layer, 0, ORDER[0][0], 0)
                norm_lo(layer, 0, 1)
                ffn_lo(layer, 0, ORDER[0][1], 0)
                ffn(layer, 0)
                mix_lo(layer, 0)
                residual(layer, 0, 0)
                norm_scale(layer, 1, 0)
                residual(layer, 0, 1)
                norm_scale(layer, 1, 1)
                norm_lo(layer, 1, 0)
                norm_lo(layer, 1, 1)
                mix_lo(layer, 1)
                mix_lo(layer, 2)
                dve.wait_ge(*params(layer, NPAR))
                dve.tensor_scalar(p_half[:], p_vec[:, 0:2, :], 0.5, None, ALU.mult).then_inc(params_pool.sem, 1)
                dve.tensor_scalar(p_1mka[:], p_vec[:, 3, :], -1.0, 1.0, ALU.mult, ALU.add) \
                    .then_inc(params_pool.sem, 1)
                dve.wait_ge(*params_pool(layer, 2))
                dve.wait_ge(consts_ready, 1)
                mixer(layer)
                residual(layer, 1, 0)
                residual(layer, 1, 1)
                norm_scale(layer, 2, 0)
                norm_scale(layer, 2, 1)
                norm_lo(layer, 2, 0)
                norm_lo(layer, 2, 1)
                ffn_lo(layer, 1, ORDER[1][1], 0)
                ffn(layer, 1)
                residual(layer, 2, 0)
                norm_scale(layer + 1, 0, 0)
                residual(layer, 2, 1)
            dve_chain.ended()
            norm_scale(DEPTH, 0, 1)

        @block.tensor
        def _(pe):
            def parts(out_, w_parts, x_parts, w_at, x_at, first, last, w_stationary):
                w, a = [t[w_at] for t in w_parts], [t[x_at] for t in x_parts]
                for n, (i, j) in enumerate(((0, 0), (0, 1), (1, 0))):
                    lhs, rhs_ = (w[i], a[j]) if w_stationary else (a[i], w[j])
                    ins = pe.matmul(out_, lhs, rhs_, start=first and n == 0, stop=last and n == 2)
                return ins

            def weights(slot, n, width):
                return [block3(t[slot], n, width) for t in (w_hi, w_lo)]

            act_parts = [act_hi[:], act_lo[:]]
            ALL = slice(None)

            def feature_major(slot, width, col, m, out_):
                for k in range(KT):
                    ins = parts(out_, weights(slot, KT, width), act_parts,
                                (ALL, k, slice(col, col + m)), (ALL, k, ALL), k == 0, k == KT - 1, True)
                return ins

            Y_SIGNALS = ((0, 1), (1, 0))

            def tile_of(t):
                return slice(t * P, (t + 1) * P)

            def token_major(slot, width, col, n, t, out_):
                for k in range(KT):
                    ins = parts(out_, weights(slot, KT, width), act_parts, (ALL, k, slice(col, col + n)),
                                (ALL, k, slice(t * P, (t + 1) * P)), k == 0, k == KT - 1, False)
                return ins

            def keep_warm(n, out_):
                for _ in range(n):
                    pe.matmul(out_[:, 0:P], ident[:], ident[:], start=True, stop=True)

            def norm_turn(layer, norm, t):
                for b in range(2):
                    pe.wait_ge(*xs_ready(layer, norm * HALVES + 2 * t + b + 1))
                    for k in range(4):
                        ins = pe.transpose(TR_B[2 * t + b][:, k * P:(k + 1) * P],
                                           xs[:, t, (4 * b + k) * P:(4 * b + k + 1) * P], ident[:])
                    ins.then_inc(xt_ready.sem, 1)

            def turn_normed(layer, norm):
                waits = (6, 1, 6) if norm == 2 else (0, 12, 5)
                keep_warm(waits[0], bank[1])
                norm_turn(layer, norm, 0)
                keep_warm(waits[1], bank[2])
                norm_turn(layer, norm, 1)
                keep_warm(waits[2], bank[2])
                pe.wait_ge(*act_ready(layer, norm * 4 + 4))

            def ffn(layer, ffn):
                def product(slot, i):
                    pe.wait_ge(*split_ready[slot](layer, ffn_use(ffn, slot, i) + 1))
                    out_ = (GATE_B, up_bank(ffn, i))[slot]
                    for j in range(2):
                        ins = feature_major(slot, GW, j * P, P, out_[:, j * T:(j + 1) * T])
                    ins.then_inc(used[slot].sem, 1)

                def up_and_gate(i):
                    n = ffn * NG + i
                    for slot in ORDER[ffn]:
                        if slot == 0 or up_bank(ffn, i) is up_bank(ffn, i - 1):
                            pe.wait_ge(*(silu_ready, hid_ready)[slot](layer, n))
                        product(slot, i)

                def down(i, t, first=False, last=False):
                    slot, use = down_slot(ffn, i)
                    if t == 0:
                        pe.wait_ge(*hid_split(layer, ffn * NG + i + 1))
                        pe.wait_ge(*split_ready[slot](layer, ffn_use(ffn, slot, use) + 1))
                    for half in range(2):
                        for j in range(2):
                            ins = parts(Y_B[2 * t + half][:], weights(slot, 2, D),
                                        [last_hi, last_lo] if last else [hid_hi[:], hid_lo[:]],
                                        (ALL, j, slice(half * BANK, (half + 1) * BANK)),
                                        (ALL, TT * j + t, ALL) if last else (ALL, j, tile_of(t)),
                                        first and j == 0, last and j == 1, False)
                        if last and (t, half) in Y_SIGNALS:
                            ins.then_inc(y_ready.sem, 1)
                    if t == TT - 1:
                        ins.then_inc(used[slot].sem, 1)

                turn_normed(layer, 2 * ffn)
                for slot in ORDER[ffn]:
                    product(slot, 0)
                up_and_gate(1)
                for t in range(TT):
                    down(0, t, first=True)
                with pe.Fori(2, NG - 1) as i:
                    up_and_gate(i)
                    for t in range(TT):
                        down(i - 1, t)
                up_and_gate(NG - 1)
                for t in range(TT):
                    down(NG - 2, t)
                    down(NG - 1, t, last=True)

            def mixer(layer):
                def piece(m):
                    slot, use = mix_use(m)
                    pe.wait_ge(*split_ready[slot](layer, use + 1))
                    if m >= 2 and m < NIN:
                        pe.wait_ge(*proj_out(layer, m - 1))
                    return slot, used[slot].sem, bank[m % 2]

                def two_tiles(m):
                    slot, done, b = piece(m)
                    for j in range(2):
                        ins = feature_major(slot, 256, j * P, P, b[:, j * T:(j + 1) * T])
                    ins.then_inc(done, 1)

                turn_normed(layer, 1)
                slot, done, b = piece(0)
                width = IN_COLS[0][1]
                feature_major(slot, width, 0, P, b[:, 0:T])
                for j in range(2):
                    ins = feature_major(slot, width, P + j * GH, GH, bank[2][0:GH, j * T:(j + 1) * T])
                ins.then_inc(done, 1)
                two_tiles(1)
                two_tiles(2)
                pe.wait_ge(consts_ready, 1)
                pe.wait_ge(*params(layer, NPAR))
                pe.wait_ge(*tw_ready(layer, 1))
                for n, (w, r) in enumerate(((slice(0, LORA), tw[:]), (slice(LORA, P), xwa[LORA:P, :]))):
                    for c in range(CT):
                        ins = pe.matmul(bank[3 + n][:, c * T:(c + 1) * T], wa_up[w, c * P:(c + 1) * P], r,
                                        start=True, stop=True)
                    ins.then_inc(lora_out.sem, 1)
                two_tiles(3)
                pe.wait_ge(*kk_sq_ready(layer, 1))
                pe.matmul(bank[5][:], head_ones[:], kk_sq[:].rearrange("p c t -> p (c t)"), start=True,
                          stop=True).then_inc(kk_sum.sem, 1)
                two_tiles(4)
                two_tiles(5)
                pe.wait_ge(*mixed(layer, 5))
                for q in range(TT):
                    for c in range(CT):
                        ins = pe.transpose(bank[5][:, q * C + c * P:q * C + (c + 1) * P],
                                           vx[:, c, q * P:(q + 1) * P], ident[:])
                ins.then_inc(v_out.sem, 1)
                pe.wait_ge(*sig_g_ready(layer, 1))
                for q in range(TT):
                    for j in range(2):
                        ins = pe.matmul(bank[2][:, q * C:(q + 1) * C], sig_g[:, j, q * P:(q + 1) * P],
                                        g_up[:, j, :], start=(j == 0), stop=(j == 1))
                ins.then_inc(g_out.sem, 1)
                slot, done, b = piece(6)
                for t in range(TT):
                    ins = token_major(slot, 256, 0, SB, t, b[:, t * SB:(t + 1) * SB])
                ins.then_inc(done, 1)
                two_tiles(7)
                pe.wait_ge(*chan_ready(layer, 1))
                for q in range(TT):
                    for c in range(CT):
                        ins = pe.matmul(bank[4][:, q * NH + 2 * c:q * NH + 2 * c + 2],
                                        rkk[:, c, q * P:(q + 1) * P], head_of[:], start=True, stop=True)
                ins.then_inc(bonus_out.sem, 1)
                for n, t in enumerate((bm, km)):
                    for c in range(CT):
                        ins = pe.transpose(bank[3][:, n * C + c * P:n * C + (c + 1) * P], t[:, c * TT, :],
                                           ident[:])
                ins.then_inc(bk_out.sem, 1)
                two_tiles(8)

                def head(n):
                    q, h = n // NH, n % NH
                    return q, h, slice(HD * (h % 2), HD * (h % 2) + HD), (h // 2) * TT + q

                pe.wait_ge(*bk_ready(layer, 1))
                pe.wait_ge(*g_ready(layer, 1))
                for n in range(TT * NH):
                    q, h, ch, i = head(n)
                    if n >= 2:
                        pe.wait_ge(*pair_ready(layer, n - 1))
                    both = ar[ch, i, :, :].rearrange("p a t -> p (a t)")
                    pe.matmul(bank[2 + n % 2][:, 0:2 * P], bm[ch, i, :], both, start=True, stop=True)
                    pe.matmul(bank[2 + n % 2][:, 2 * P:], km[ch, i, :], both, start=True, stop=True) \
                        .then_inc(pair_out.sem, 1)
                pe.wait_ge(*bonus_ready(layer, 1))
                pe.wait_ge(*v_ready(layer, 1))
                for n in range(TT * NH):
                    q, h, ch, i = head(n)
                    b = q * CT + h // 2
                    ins = pe.matmul(bank[4 + h % 2][:, b * P:(b + 1) * P], ar[ch, i, 0, :], bm[ch, i, :],
                                    start=True, stop=True)
                ins.then_inc(low_out.sem, 1)
                def sb_z(h):
                    c, ch, z = h // 2, slice(HD * (h % 2), HD * (h % 2) + HD), bank[6 + h % NZ]
                    if h < NZ:
                        pe.wait_ge(*proj_out(layer, 6))
                    else:
                        pe.wait_ge(*arg_ready(layer, h + 1 - NZ))
                    pe.matmul(z[:, 0:T], sbk[ch, c, 0:P], sbq[ch, c, :], start=True, stop=True)
                    pe.matmul(z[:, T:3 * P], sbk[ch, c, P:T], sbq[ch, c, P:T], start=True, stop=True) \
                        .then_inc(sbz_out.sem, 1)

                for h in range(NZ):
                    sb_z(h)
                slot, _, b = piece(9)
                feature_major(slot, 256, 0, P, b[:, 0:T]).then_inc(swk_out.sem, 1)

                def sw_v(t):
                    slot, _ = mix_use(9)
                    ins = token_major(slot, 256, P, P, t, bank[1][:, T + t * P:T + (t + 1) * P])
                    if t == TT - 1:
                        ins.then_inc(used[slot].sem, 1)

                def sb_inclusive(h):
                    i = h % NZ
                    z = bank[6 + i]
                    pe.wait_ge(*sp_ready(layer, h + 1))
                    pe.matmul(z[:, 0:3 * P], suffix[:], sp_m[:, i, :], start=True, stop=False)
                    pe.matmul(z[:, P:T], ones[:], sp_m[:, i, T:3 * P], start=False, stop=True) \
                        .then_inc(sbi_out.sem, 1)

                def values(out_, v0, v1, probs):
                    pe.matmul(out_[:, 0:T], v0, probs[:, 0:T], start=True, stop=False)
                    return pe.matmul(out_[:, P:T], v1, probs[:, T:3 * P], start=False, stop=True)

                def sb_values(h):
                    ch = slice(HD * (h % 2), HD * (h % 2) + HD)
                    pe.wait_ge(*sbw_ready(layer, h + 1))
                    d = slice(h * HD, (h + 1) * HD)
                    values(bank[0][ch, (h // 2) * T:(h // 2 + 1) * T], sbv[:, 0, d], sbv[:, 1, d],
                           sb_w[:, h % NZ, :]).then_inc(sbo_out.sem, 1)

                def sw_z(h):
                    tile, ch, z = h // 2, slice(HD * (h % 2), HD * (h % 2) + HD), bank[6 + h % NZ]
                    k = swk[ch, 0 if h // GRP == h % 2 else 1, :]
                    if h < NZ:
                        pe.wait_ge(*arg_ready(layer, NH - NZ + h + 1))
                        pe.wait_ge(*proj_out(layer, 9))
                        pe.wait_ge(*swk_swapped(layer, 2))
                    else:
                        pe.wait_ge(*swz_ready(layer, h + 1 - NZ))
                    pe.matmul(z[:, 0:P], swq[ch, tile, 0:P], k[:, 0:P], start=True, stop=True)
                    pe.matmul(z[:, P:3 * P], swq[ch, tile, P:T], k, start=True, stop=True) \
                        .then_inc(swz_out.sem, 1)

                def sw_turn(h):
                    i = h % NZ
                    pe.wait_ge(*swp_ready(layer, h + 1))
                    if h < NZ:
                        pe.wait_ge(*swz_ready(layer, SWH))
                    else:
                        pe.wait_ge(*swt_ready(layer, h + 1 - NZ))
                    for b in range(3):
                        ins = pe.transpose(bank[6 + i][:, b * P:(b + 1) * P], sw_p[:, h, b * P:(b + 1) * P],
                                           ident[:])
                    ins.then_inc(swt_out.sem, 1)

                def sw_values(h):
                    ch, tile = slice(HD * (h % 2), HD * (h % 2) + HD), h // 2
                    d = slice((h // GRP) * HD, (h // GRP + 1) * HD)
                    pe.wait_ge(*swt_ready(layer, h + 1))
                    if h == 0:
                        pe.wait_ge(*proj_out(layer, NIN))
                    if h == 4:
                        pe.wait_ge(*pair_split(layer, 1))
                    values(bank[(1 + h // 4) % 2][ch, (tile % 2) * T:(tile % 2 + 1) * T], swv[:, 0, d], swv[:, 1, d],
                           sw_pt[:, h % NZ, :]).then_inc(swo_out.sem, 1)

                for slot in range(NSLOT):
                    lev, phase = slot // 2 + 1, slot % 2
                    for q in range(TT):
                        if slot // 2 >= len(LEVELS) - 1:
                            break
                        if phase == 0:
                            pe.wait_ge(*inv_ready(layer, (lev - 1) * TT + q + 1))
                            if lev == 1:
                                pe.wait_ge(*pair_ready(layer, TT * NH))
                            for h in range(NH):
                                n = q * NH + h
                                ins = pe.matmul(bank[2 + q][:, h * P:(h + 1) * P], pm[:, n, 0, :],
                                                inv[:, n, :], start=True, stop=True)
                            ins.then_inc(off_out.sem, 1)
                            for h in range(NH):
                                ins = pe.transpose(bank[4 + q][:, h * P:(h + 1) * P],
                                                   inv[:, q * NH + h, :], ident[:])
                            ins.then_inc(inv_turned.sem, 1)
                        else:
                            pe.wait_ge(*off_ready(layer, (lev - 1) * TT + q + 1))
                            pe.wait_ge(*inv_t_ready(layer, (lev - 1) * TT + q + 1))
                            for h in range(NH):
                                n = q * NH + h
                                if lev < len(LEVELS) - 1:
                                    ins = pe.matmul(bank[4 + q][:, h * P:(h + 1) * P], inv_t[:, n, :],
                                                    off[:, n, :], start=True, stop=True)
                                else:
                                    ins = pe.matmul(bank[2 + q][:, h * P:(h + 1) * P], off[:, n, :],
                                                    inv_t[:, n, :], start=True, stop=True)
                            ins.then_inc(inv_out.sem, 1)
                    for what, h in SLOT[slot]:
                        if what == "sbz":
                            sb_z(h)
                        elif what == "sbi":
                            sb_inclusive(h)
                        elif what == "sbv":
                            sb_values(h)
                        elif what == "v":
                            sw_v(h)
                        elif what == "swz":
                            sw_z(h)
                        elif what == "swt":
                            sw_turn(h)
                        elif what == "swv":
                            sw_values(h)

                def project_back(m, t, halves=(0, 1)):
                    slot, use = mix_use(m)
                    k0 = OUT_KT[m - NIN]
                    if t == 0:
                        pe.wait_ge(*split_ready[slot](layer, use + 1))
                    for half in halves:
                        for j in range(2):
                            ins = parts(Y_B[2 * t + half][:], weights(slot, 2, D), act_parts,
                                        (ALL, j, slice(half * BANK, (half + 1) * BANK)),
                                        (ALL, k0 + j, slice(t * P, (t + 1) * P)),
                                        m == NIN and j == 0, m == NMIX - 1 and j == 1, False)
                        if m == NMIX - 1 and (t, half) in Y_SIGNALS:
                            ins.then_inc(y_ready.sem, 1)
                    if t == TT - 1 and 1 in halves:
                        ins.then_inc(used[slot].sem, 1)

                def from_state(q, h, which, out_):
                    if q and h % 2 == 0:
                        c = h // 2
                        pe.matmul(out_[:, c * P:(c + 1) * P], ar[:, c * TT + q, which, :],
                                  s0[:, c, :, :].rearrange("p h d -> p (h d)"), start=True, stop=False)

                def solve_rhs(q):
                    if q == 0:
                        pe.wait_ge(*swt_ready(layer, SWH))
                    else:
                        pe.wait_ge(*s0_ready(layer, 1))
                    for h in range(NH):
                        d = slice(h * HD, (h + 1) * HD)
                        from_state(q, h, 0, bank[6])
                        ins = pe.matmul(bank[6][:, d], pm[:, q * NH + h, 2, :], v_tok[:, q, d], start=(q == 0),
                                        stop=(q == 0 or h % 2 == 1))
                    ins.then_inc(rhs_out.sem, 1)

                def solve(q):
                    pe.wait_ge(*rhs_ready(layer, q + 1))
                    if q:
                        pe.wait_ge(*sa_ready(layer, q))
                    for h in range(NH):
                        d = slice(h * HD, (h + 1) * HD)
                        ins = pe.matmul(bank[7][:, d], inv_t[:, q * NH + h, :], rhs[:, q, d], start=True,
                                        stop=True)
                    ins.then_inc(sa_out.sem, 1)

                def read_out(q):
                    pe.wait_ge(*sa_ready(layer, q + 1))
                    for h in range(NH):
                        n = q * NH + h
                        d = slice(h * HD, (h + 1) * HD)
                        from_state(q, h, 1, bank[q])
                        pe.matmul(bank[q][:, d], pm[:, n, 1, :], sa[:, q, d], start=(q == 0), stop=False)
                        ins = pe.matmul(bank[q][:, d], pm[:, n, 3, :], v_tok[:, q, d], start=False,
                                        stop=(q == 0 or h % 2 == 1))
                    ins.then_inc(yr_out.sem, 1)

                def next_state():
                    pe.wait_ge(*sa_ready(layer, 1))
                    for h in range(NH):
                        ch, d = slice(HD * (h % 2), HD * (h % 2) + HD), slice(h * HD, (h + 1) * HD)
                        o = bank[1][ch, BANK - C + (h // 2) * HD:BANK - C + (h // 2 + 1) * HD]
                        pe.matmul(o, bk_tok[:, 0, d], sa[:, 0, d], start=True, stop=False)
                        ins = pe.matmul(o, bk_tok[:, 1, d], v_tok[:, 0, d], start=False, stop=True)
                    ins.then_inc(s0_out.sem, 1)

                def turn_heads(q):
                    pe.wait_ge(*yr_ready(layer, q + 1))
                    if q == 0:
                        pe.wait_ge(*rhs_ready(layer, TT))
                    for c in range(CT):
                        ins = pe.transpose(bank[6 + q][:, c * P:(c + 1) * P], y_c[:, q, c * P:(c + 1) * P],
                                           ident[:])
                    ins.then_inc(rwt_out.sem, 1)

                solve_rhs(0)
                pe.wait_ge(*inv_ready(layer, TT * len(LEVELS)))
                project_back(10, 0, [0])
                solve(0)
                project_back(10, 0, [1])
                pe.wait_ge(*pair_split(layer, TILE_PAIRS - 1))
                next_state()
                pe.wait_ge(*pair_split(layer, TILE_PAIRS))
                read_out(0)
                project_back(10, 1, [0])
                solve_rhs(1)
                project_back(10, 1, [1])
                solve(1)
                project_back(11, 0, [0])
                read_out(1)
                project_back(11, 0, [1])
                project_back(11, 1)
                project_back(12, 0)
                turn_heads(0)
                project_back(12, 1)
                pe.wait_ge(*rwt_split(layer, 1))
                project_back(13, 0, [0])
                turn_heads(1)
                project_back(13, 0, [1])
                pe.wait_ge(*rwt_split(layer, 2))
                project_back(13, 1)

            pe.wait_ge(ident_ready, 1)
            keep_warm(16, bank[1])
            with pe.Fori(0, DEPTH) as layer:
                ffn(layer, 0)
                mixer(layer)
                ffn(layer, 1)


SLOT = [
    [("sbi", 0), ("sbi", 1)],
    [("sbz", 2), ("sbz", 3), ("sbv", 0), ("sbv", 1)],
    [("sbi", 2), ("sbi", 3), ("hi", 12)],
    [("sbv", 2), ("sbv", 3), ("swz", 0), ("swz", 1)],
    [("lo", 12), ("swz", 2), ("swz", 3)],
    [("swz", 4), ("swz", 5)],
    [("swz", 6), ("swz", 7), ("swmax", 0)],
    [("swe", 0), ("swe", 1), ("swe", 2), ("swe", 3), ("v", 0)],
    [("swn", 0), ("swe", 4), ("swe", 5), ("swe", 6), ("swe", 7), ("v", 1), ("swt", 0), ("swt", 1),
     ("sbout", 0)],
    [("swn", 1), ("swv", 0), ("swv", 1), ("swt", 2), ("swt", 3), ("hi", 11)],
    [("swv", 2), ("swv", 3), ("swout", 0), ("swt", 4), ("swt", 5), ("lo", 11)],
    [("swv", 4), ("swv", 5), ("swt", 6), ("swt", 7), ("swv", 6), ("swv", 7), ("swout", 1)],
]
NSLOT = len(SLOT)


_INS = ["x", "ffn1_norm", "ffn1_w_in", "ffn1_w_out", "mix_norm", "mix_w_in", "mix_w_out", "rw_mu", "rw_w0",
        "rw_w_up", "rw_a0", "rw_a_up", "rw_g_up", "rw_k_k", "rw_k_a", "rw_r_k", "rw_gn_g", "rw_gn_b",
        "sw_sinks", "ffn2_norm", "ffn2_w_in", "ffn2_w_out", "final_norm"]


def kernel(**inputs):
    import numpy as np
    import concourse.bacc as bacc
    from concourse.bass_utils import run_bass_kernel_spmd

    nc = bacc.Bacc("TRN2", target_bir_lowering=False, num_devices=1)
    arrays, args = {}, []
    for name in _INS:
        a = np.ascontiguousarray(inputs[name])
        arrays[f"in_{name}"] = a
        args.append(nc.dram_tensor(f"in_{name}", a.shape, mybir.dt.from_np(a.dtype), kind="ExternalInput").ap())
    x = arrays["in_x"]
    args.append(nc.dram_tensor("out_y", x.shape, mybir.dt.from_np(x.dtype), kind="ExternalOutput").ap())
    hybrid_trunk(nc, *args)
    r = run_bass_kernel_spmd(nc, [arrays], core_ids=[0])
    return r.results[0]["out_y"]
```
